# Optimizing a Trainium2 kernel written in Bass

```python
import math
import jax, jax.numpy as jnp
from jax import lax
import numpy as np

D_MODEL = 1024
BATCH = 1
SEQ = 256
DEPTH = 1

HEAD_DIM = 64
N_HEADS_SB = 8
N_HEADS_MOBA = 8
D_SB = N_HEADS_SB * HEAD_DIM
D_MOBA = N_HEADS_MOBA * HEAD_DIM
SB_Q_BLOCK = 128
MOBA_BLOCK = 256
MOBA_TOPK = 3
MOBA_Q_CHUNK = 16
REL_BUCKETS = 32
REL_MAX_DIST = 128
N_EXPERTS = 32
TOP_K = 4
D_EXPERT = D_MODEL
SWIGLU_LIMIT = 7.0
SWIGLU_ALPHA = 1.702
RMS_EPS = 1e-6
IN_SPLIT_POINTS = (D_SB, 2 * D_SB, 3 * D_SB, 3 * D_SB + D_MOBA, 3 * D_SB + 2 * D_MOBA, 3 * D_SB + 3 * D_MOBA, 3 * D_SB + 3 * D_MOBA + D_MODEL)
D_IN_PROJ = 3 * D_SB + 3 * D_MOBA + 2 * D_MODEL

kernel_name = "hybrid_stickbreak_moba_moe_block"

def rmsnorm(x, g):
    xf = x.astype(jnp.float32)
    var = jnp.mean(xf * xf, axis=-1, keepdims=True)
    return (xf * lax.rsqrt(var + RMS_EPS)).astype(x.dtype) * g

def split_heads(t, n_heads):
    B, S, _ = t.shape
    return t.reshape(B, S, n_heads, HEAD_DIM).transpose(0, 2, 1, 3)

def merge_heads(t):
    B, H, S, dh = t.shape
    return t.transpose(0, 2, 1, 3).reshape(B, S, H * dh)

def rel_bucket(dist):
    n = jnp.maximum(dist, 0)
    max_exact = REL_BUCKETS // 2
    nf = jnp.maximum(n, 1).astype(jnp.float32)
    large = max_exact + (jnp.log(nf / max_exact) / math.log(REL_MAX_DIST / max_exact)
                         * (REL_BUCKETS - max_exact)).astype(jnp.int32)
    large = jnp.minimum(large, REL_BUCKETS - 1)
    return jnp.where(n < max_exact, n, large)

def stick_breaking_attention(q, k, v):
    B, H, S, dh = q.shape
    nq = S // SB_Q_BLOCK
    qb = q.reshape(B, H, nq, SB_Q_BLOCK, dh).transpose(2, 0, 1, 3, 4)
    key_pos = jnp.arange(S)
    scale = 1.0 / math.sqrt(dh)

    def block(args):
        i, qi = args
        q_pos = i * SB_Q_BLOCK + jnp.arange(SB_Q_BLOCK)
        z = jnp.einsum('bhqd,bhkd->bhqk', qi, k).astype(jnp.float32) * scale
        causal = key_pos[None, :] < q_pos[:, None]
        log_keep = jnp.where(causal, -jax.nn.softplus(z), 0.0)
        tail = lax.cumsum(log_keep, axis=3, reverse=True) - log_keep
        a = jnp.where(causal, jnp.exp(jax.nn.log_sigmoid(z) + tail), 0.0)
        return jnp.einsum('bhqk,bhkd->bhqd', a.astype(v.dtype), v)

    out = lax.map(block, (jnp.arange(nq), qb))
    return out.transpose(1, 2, 0, 3, 4).reshape(B, H, S, dh)

_gather_blocks = jax.vmap(jax.vmap(lambda blk, idx: blk[idx]))

def moba_attention(q, k, v, rel_bias):
    B, H, S, dh = q.shape
    L = MOBA_BLOCK
    n_blk = -(-S // L)
    pad = n_blk * L - S
    kp = jnp.pad(k, ((0, 0), (0, 0), (0, pad), (0, 0)))
    vp = jnp.pad(v, ((0, 0), (0, 0), (0, pad), (0, 0)))
    k_blocks = kp.reshape(B, H, n_blk, L, dh)
    v_blocks = vp.reshape(B, H, n_blk, L, dh)
    k_mean = jnp.mean(k_blocks.astype(jnp.float32), axis=3)
    k_sel = min(MOBA_TOPK, n_blk)
    scale = 1.0 / math.sqrt(dh)
    C = MOBA_Q_CHUNK
    nq = S // C
    qc = q.reshape(B, H, nq, C, dh).transpose(2, 0, 1, 3, 4)
    offs = jnp.arange(L)
    rel_t = rel_bias.T
    head_idx = jnp.arange(H)[:, None, None, None]

    def chunk(args):
        i, qi = args
        q_pos = i * C + jnp.arange(C)
        own_blk = (i * C) // L
        gs = jnp.einsum('bhqd,bhnd->bhqn', qi.astype(jnp.float32), k_mean)
        past = jnp.arange(n_blk) < own_blk
        gs = jnp.where(past[None, None, None, :], gs, -jnp.inf)
        _, top = lax.top_k(gs, k_sel)
        sel_valid = top < own_blk
        kg = _gather_blocks(k_blocks, top)
        vg = _gather_blocks(v_blocks, top)
        s_past = jnp.einsum('bhqd,bhqmld->bhqml', qi, kg).astype(jnp.float32) * scale
        dist_past = q_pos[None, None, :, None, None] - (top[..., None] * L + offs)
        bias_past = rel_t[head_idx, rel_bucket(dist_past)]
        s_past = jnp.where(sel_valid[..., None], s_past + bias_past, -jnp.inf)
        k_own = lax.dynamic_slice_in_dim(k_blocks, own_blk, 1, axis=2)[:, :, 0]
        v_own = lax.dynamic_slice_in_dim(v_blocks, own_blk, 1, axis=2)[:, :, 0]
        s_own = jnp.einsum('bhqd,bhld->bhql', qi, k_own).astype(jnp.float32) * scale
        dist_own = q_pos[:, None] - (own_blk * L + offs)[None, :]
        bias_own = rel_t[:, rel_bucket(dist_own)]
        s_own = jnp.where((dist_own >= 0)[None, None], s_own + bias_own[None], -jnp.inf)
        scores = jnp.concatenate([s_past.reshape(B, H, C, k_sel * L), s_own], axis=-1)
        p = jax.nn.softmax(scores, axis=-1).astype(v.dtype)
        p_past = p[..., :k_sel * L].reshape(B, H, C, k_sel, L)
        p_own = p[..., k_sel * L:]
        return (jnp.einsum('bhqml,bhqmld->bhqd', p_past, vg)
                + jnp.einsum('bhql,bhld->bhqd', p_own, v_own))

    out = lax.map(chunk, (jnp.arange(nq), qc))
    return out.transpose(1, 2, 0, 3, 4).reshape(B, H, S, dh)

def moe_ffn(x, w_router, b_router, w_gate_up, b_gate_up, w_down, b_down):
    B, S, D = x.shape
    xt = x.reshape(B * S, D)
    logits = (xt @ w_router + b_router).astype(jnp.float32)
    top_val, top_idx = lax.top_k(logits, TOP_K)
    top_w = jax.nn.softmax(top_val, axis=-1)
    gates = jnp.sum(jax.nn.one_hot(top_idx, N_EXPERTS, dtype=jnp.float32) * top_w[..., None], axis=1)

    def expert_step(acc, params):
        wgu, bgu, wd, bd, g = params
        hgu = xt @ wgu + bgu
        gate = jnp.minimum(hgu[:, :D_EXPERT], SWIGLU_LIMIT)
        up = jnp.clip(hgu[:, D_EXPERT:], -SWIGLU_LIMIT, SWIGLU_LIMIT)
        y = ((up + 1.0) * (gate * jax.nn.sigmoid(SWIGLU_ALPHA * gate))) @ wd + bd
        return acc + g[:, None].astype(y.dtype) * y, None

    acc, _ = lax.scan(expert_step, jnp.zeros_like(xt), (w_gate_up, b_gate_up, w_down, b_down, gates.T))
    return acc.reshape(B, S, D)

def setup_inputs(seed: int = 0) -> dict:
    key = jax.random.key(seed)
    ks = jax.random.split(key, 15)
    f32 = jnp.float32
    nrm = lambda k, shape, s: jax.random.normal(k, shape, f32) * s
    return {
        "x": nrm(ks[0], (BATCH, SEQ, D_MODEL), 1.0),
        "norm_mix_g": 1.0 + nrm(ks[1], (DEPTH, D_MODEL), 0.02),
        "w_in": nrm(ks[2], (DEPTH, D_MODEL, D_IN_PROJ), D_MODEL ** -0.5),
        "w_proj_sb": nrm(ks[3], (DEPTH, D_SB, D_MODEL), D_SB ** -0.5),
        "w_proj_moba": nrm(ks[4], (DEPTH, D_MOBA, D_MODEL), D_MOBA ** -0.5),
        "w_out": nrm(ks[5], (DEPTH, D_MODEL, D_MODEL), D_MODEL ** -0.5),
        "rel_bias": nrm(ks[6], (REL_BUCKETS, N_HEADS_MOBA), 0.5),
        "norm_ffn_g": 1.0 + nrm(ks[7], (DEPTH, D_MODEL), 0.02),
        "w_router": nrm(ks[8], (DEPTH, D_MODEL, N_EXPERTS), D_MODEL ** -0.5),
        "b_router": nrm(ks[9], (DEPTH, N_EXPERTS), 0.01),
        "w_gate_up": nrm(ks[10], (DEPTH, N_EXPERTS, D_MODEL, 2 * D_EXPERT), D_MODEL ** -0.5),
        "b_gate_up": nrm(ks[11], (DEPTH, N_EXPERTS, 2 * D_EXPERT), 0.02),
        "w_down": nrm(ks[12], (DEPTH, N_EXPERTS, D_EXPERT, D_MODEL), D_EXPERT ** -0.5),
        "b_down": nrm(ks[13], (DEPTH, N_EXPERTS, D_MODEL), 0.02),
        "norm_final_g": 1.0 + nrm(ks[14], (D_MODEL,), 0.02),
    }

def reference(x, norm_mix_g, w_in, w_proj_sb, w_proj_moba, w_out, rel_bias, norm_ffn_g,
              w_router, b_router, w_gate_up, b_gate_up, w_down, b_down, norm_final_g):
    h = x
    for l in range(DEPTH):
        xn = rmsnorm(h, norm_mix_g[l])
        proj = xn @ w_in[l]
        q_sb, k_sb, v_sb, q_mb, k_mb, v_mb, g_sb, g_mb = jnp.split(proj, IN_SPLIT_POINTS, axis=-1)
        y_sb = stick_breaking_attention(split_heads(q_sb, N_HEADS_SB), split_heads(k_sb, N_HEADS_SB),
                                        split_heads(v_sb, N_HEADS_SB))
        y_mb = moba_attention(split_heads(q_mb, N_HEADS_MOBA), split_heads(k_mb, N_HEADS_MOBA),
                              split_heads(v_mb, N_HEADS_MOBA), rel_bias)
        merged = (jax.nn.sigmoid(g_sb) * (merge_heads(y_sb) @ w_proj_sb[l])
                  + jax.nn.sigmoid(g_mb) * (merge_heads(y_mb) @ w_proj_moba[l]))
        h = h + merged @ w_out[l]
        hn = rmsnorm(h, norm_ffn_g[l])
        h = h + moe_ffn(hn, w_router[l], b_router[l], w_gate_up[l], b_gate_up[l], w_down[l], b_down[l])
    return rmsnorm(h, norm_final_g)


_drawn_inputs = setup_inputs


def setup_inputs(seed=0):
    import zlib

    import numpy as np

    out = dict(_drawn_inputs(seed))
    spreads = {}
    factors = {'b_gate_up': 5.383, 'b_down': 6.134, 'norm_final_g': 2.876}
    for name, (base, spread) in spreads.items():
        noise = np.random.default_rng([zlib.crc32(name.encode()), seed]).standard_normal(out[name].shape)
        drawn = base * np.exp(spread * noise) if base else spread * noise
        out[name] = __import__('jax').numpy.asarray(drawn.astype(out[name].dtype))
    for name, factor in factors.items():
        out[name] = (out[name] * factor).astype(out[name].dtype)
    return out
```

```python
from contextlib import ExitStack

import numpy as np

import concourse.bass as bass
from concourse import mybir

ALU = mybir.AluOpType
ACT = mybir.ActivationFunctionType
F32 = mybir.dt.float32
BF16 = mybir.dt.bfloat16
I32 = mybir.dt.int32
U32 = mybir.dt.uint32
AX_X = mybir.AxisListType.X

P = 128
HEAD_DIM = 64
REL_MAX_DIST = 128
TOP_K = 4
SWIGLU_LIMIT = 7.0
SWIGLU_ALPHA = 1.702
RMS_EPS = 1e-6
MASKED = -1.0e30
SLOTS = 64


def bucket_rows(buckets, width):
    dist = np.arange(width) - (P - 1)
    n = np.maximum(dist, 0)
    exact = buckets // 2
    ratio = np.log(np.maximum(n, 1).astype(np.float64) / exact) / np.log(REL_MAX_DIST / exact)
    large = np.minimum(exact + (ratio * (buckets - exact) + 1e-9).astype(np.int64), buckets - 1)
    bucket = np.where(n < exact, n, large)
    rows = (np.arange(buckets)[:, None] == bucket[None, :]) & (dist >= 0)[None, :]
    return rows.astype(np.float32)


def hybrid_layer(nc, x, norm_mix_g, w_in, w_proj_sb, w_proj_moba, w_out, rel_bias, norm_ffn_g,
                 w_router, b_router, w_gate_up, b_gate_up, w_down, b_down, norm_final_g,
                 bucket_onehot, out):
    D = x.shape[2]
    T = x.shape[1]
    NT = T // P
    KD = D // P
    HSB = w_proj_sb.shape[1] // HEAD_DIM
    HMB = w_proj_moba.shape[1] // HEAD_DIM
    NH = HSB + HMB
    HALF = D // 2
    E = w_router.shape[2]
    BUCKETS = rel_bias.shape[0]
    UW = bucket_onehot.shape[1]
    SCALE = HEAD_DIM ** -0.5
    RING = 12
    SLOT = 2 * D
    CH = 512
    NCH = w_in.shape[2] // CH
    TRI = 3 * P
    assert NT == 2 and KD == 8 and HSB == 8 and HMB == 8 and NCH == 10 and E == 32 and CH == HALF

    Q_SB, K_SB, V_SB, Q_MB, K_MB, V_MB = range(6)
    units = [("T", Q_SB, j) for j in range(4)] + [("T", K_SB, j) for j in range(4)]
    units += [("N", V_SB, t) for t in range(NT)]
    lead = len(units)
    first_fill = [("T", Q_MB, j) for j in range(4)] + [("T", K_MB, j) for j in range(4)]
    first_fill += [("N", c, t) for c in range(6, NCH) for t in range(NT)]
    second_fill = {3: ("N", V_MB, 0), 6: ("N", V_MB, 1)}
    fill_at, second_at = {}, {}
    for s in range(NH):
        fill_at[s] = len(units)
        units.append(first_fill[s])
        if s in second_fill:
            second_at[s] = len(units)
            units.append(second_fill[s])
    unit_no = {u: n for n, u in enumerate(units)}
    NU = len(units)

    PLACE = {c: c % 6 for c in range(NCH)}
    LAST_UNIT = {c: max(n for n, u in enumerate(units) if u[1] == c) for c in range(NCH)}

    ctx = ExitStack()
    with ctx:
        def sb(name, shape, dt=F32):
            return ctx.enter_context(nc.sbuf_tensor(name, shape, dt))

        def sem(name):
            return ctx.enter_context(nc.semaphore(name))

        bank = [ctx.enter_context(nc.psum_tensor(f"bank{i}", [P, 512], F32)) for i in range(8)]

        ring = sb("ring", [P, RING, SLOT])
        resid = sb("resid", [P, NT, D])
        scaled = sb("scaled", [P, NT, D])
        colsT = sb("colsT", [P, KD, T])
        qkT = sb("qkT", [P, 16, T])
        values = sb("values", [P, NT, D])
        gates = sb("gates", [P, NT, 2 * D])
        bias = sb("bias", [P, HMB, T])
        yT = sb("yT", [P, NH // 2, T])
        att_a = sb("att_a", [P, 2, TRI])
        att_e = sb("att_e", [P, 2, TRI])
        att_s = sb("att_s", [P, 2, TRI])
        att_w = sb("att_w", [P, 2, TRI])
        gfin = sb("gfin", [P, D])
        bgu = sb("bgu", [3 * E, 2 * D], BF16)
        slot_no = sb("slot_no", [P, NT, P])
        onehot_w = sb("onehot_w", [P, NT, P])
        onehot_g = sb("onehot_g", [P, NT, P])
        onehot = sb("onehot", [P, NT, SLOTS], BF16)
        scatter_w = sb("scatter_w", [P, NT, P])
        router_w = sb("router_w", [P, KD, E])
        ident = sb("ident", [P, P])
        neg_tri = sb("neg_tri", [P, P])
        neg_one = sb("neg_one", [P, P])
        before = sb("before", [P, P], BF16)
        ones_bf = sb("ones_bf", [P, P], BF16)
        expert_row = sb("expert_row", [3 * E, E + 1], BF16)
        expert_sel = sb("expert_sel", [3 * E, SLOTS], BF16)
        grow = sb("grow", [2 * KD, P])
        gcol = sb("gcol", [P, 2 * KD])
        stat = sb("stat", [P, 64])
        rel_sb = sb("rel_sb", [BUCKETS, HMB])
        b_rout = sb("b_rout", [E, 1])
        mx = sb("mx", [P, 2, 2])
        nmx = sb("nmx", [P, 2, 2])
        rs = sb("rs", [P, 2, 2])
        rr = sb("rr", [P, 2, 2])
        rout = sb("rout", [P, NT, E])
        sel = sb("sel", [P, NT, E])
        selb = sb("selb", [P, NT, E], BF16)
        gate_w = sb("gate_w", [P, NT, E])
        pick = sb("pick", [P, NT, E])
        rank = sb("rank", [P, NT, E + 1])
        gate_p = sb("gate_p", [P, NT, E + 1])
        eno = sb("eno", [P, E])
        top = sb("top", [P, NT, 8])
        topi = sb("topi", [P, NT, 8], U32)
        topf = sb("topf", [P, NT, 8])
        topp = sb("topp", [P, NT, 8])
        cnt_i = sb("cnt_i", [P, 1], I32)
        cnt_f = sb("cnt_f", [P, 1])

        pieces = [qkT[:, 4 * i:4 * i + 4, :].bitcast(BF16).rearrange("p a b -> p (a b)")
                  .rearrange("p (t d) -> p t d", t=NT) for i in range(3)]
        gate_t = gates[:, 0, 0:CH]
        sig_t = gates[:, 0, CH:2 * CH]
        up_t = gates[:, 0, 2 * CH:3 * CH]
        h_t = gates[:, 0, 3 * CH:4 * CH]
        y_t = gates[:, 1, 0:CH]
        xeT = gates[:, 1, CH:2 * CH].rearrange("p (k s) -> p k s", k=KD)
        hT = gates[:, 1, 2 * CH:3 * CH].rearrange("p (c s) -> p c s", c=4)
        gateT = yT[0:E, 0, :]
        hot_sb = att_w[0:BUCKETS, 0, :]
        u_sb = att_e[0:HMB, 0, :]
        logitT = yT[0:E, 1, :]
        bdown_sb = bias[0:E, 0:4, :].rearrange("p a b -> p (a b)")
        res2 = values[:, :, :]
        chosen = att_a[:, :, :].rearrange("p a b -> p (a b)")[:, 0:NT * TOP_K * E].rearrange(
            "p (t j e) -> p t j e", t=NT, j=TOP_K)
        u_dram = nc.dram_tensor("u_scratch", (HMB, UW), F32, kind="Internal").ap()

        def chunk_w(c):
            u = PLACE[c]
            return ring[:, 2 * u:2 * u + 2, :].rearrange("p a b -> p (a b)").rearrange("p (k n) -> p k n", k=KD)

        def flat(u0, u1):
            return ring[:, 2 * u0:2 * u1, :].rearrange("p a b -> p (a b)")

        wp_sb = flat(4, 5).rearrange("p (k n) -> p k n", k=4)
        wp_mb = flat(5, 6).rearrange("p (k n) -> p k n", k=4)
        wo_sb = flat(0, 2).rearrange("p (k n) -> p k n", k=KD)

        x_in = sem("x_in")
        x_in2 = sem("x_in2")
        small_in = sem("small_in")
        late_in = sem("late_in")
        chunk_in = [sem(f"chunk_in{c}") for c in range(NCH)]
        proj_in = sem("proj_in")
        wout_in = sem("wout_in")
        slot_in = [sem(f"slot_in{s}") for s in range(RING)]
        consts = sem("consts")
        consts2 = sem("consts2")
        gcol_ps = sem("gcol_ps")
        gcol_rd = sem("gcol_rd")
        u_ps = sem("u_ps")
        u_rd = sem("u_rd")
        u_out = sem("u_out")
        bias_in = sem("bias_in")
        ssq = sem("ssq")
        rms_var = sem("rms_var")
        rms_std = sem("rms_std")
        scaled_rd = sem("scaled_rd")
        trans_ps = sem("trans_ps")
        cols_rd = sem("cols_rd")
        cols_act = sem("cols_act")
        unit_ps = sem("unit_ps")
        unit_rd = sem("unit_rd")
        z_ps = sem("z_ps")
        ln_rd = sem("ln_rd")
        softplus = sem("softplus")
        keep_rd = sem("keep_rd")
        mid_ps = sem("mid_ps")
        weight_raw = sem("weight_raw")
        weights_rd = sem("weights_rd")
        probT_rd = sem("probT_rd")
        score_rd = sem("score_rd")
        prob_raw = sem("prob_raw")
        prob_rd = sem("prob_rd")
        pv_ps = sem("pv_ps")
        pv_rd = sem("pv_rd")
        sigm_rd = sem("sigm_rd")
        out_ps = sem("out_ps")
        merged = sem("merged")
        hres_rd = sem("hres_rd")
        logit_ps = sem("logit_ps")
        logit_rd = sem("logit_rd")
        logit2_ps = sem("logit2_ps")
        top_rd = sem("top_rd")
        pexp = sem("pexp")
        routed = sem("routed")
        weighted = sem("weighted")
        rank_ps = sem("rank_ps")
        gateT_ps = sem("gateT_ps")
        gateT_rd = sem("gateT_rd")
        count_rd = sem("count_rd")
        piece_rd = sem("piece_rd")
        piece_d = sem("piece_d")
        onehot_rd = sem("onehot_rd")
        weighted_rd = sem("weighted_rd")
        sel_rd = sem("sel_rd")
        gathered = sem("gathered")
        xe_rd = sem("xe_rd")
        slot_used = sem("slot_used")
        gate_rd = sem("gate_rd")
        sig_rd = sem("sig_rd")
        h_rd = sem("h_rd")
        hT_ps = sem("hT_ps")
        hT_rd = sem("hT_rd")
        gT_ps = sem("gT_ps")
        gT_rd = sem("gT_rd")
        y_rd = sem("y_rd")
        scattered = sem("scattered")
        dve_step = sem("dve_step")
        act_step = sem("act_step")
        pool_step = sem("pool_step")
        pass_step = sem("pass_step")
        pass_base = sem("pass_base")
        out_rd = sem("out_rd")
        out_done = sem("out_done")

        block = ctx.enter_context(nc.Block())

        def more_passes(eng, body):
            eng.wait_ge(count_rd, 1)
            largest = eng.value_load(cnt_i[0:1, 0:1], min_val=0, max_val=T)
            with eng.Fori(1, T // SLOTS) as r:
                with eng.If(largest > r * SLOTS):
                    body(r)

        @block.sync
        def _(sp):
            xt = x[0].rearrange("(t p) d -> p t d", p=P)

            def load_chunk(c):
                sp.dma_start(chunk_w(c), w_in[0].rearrange("(k p) n -> p k n", p=P)[:, :, c * CH:(c + 1) * CH]
                             ).then_inc(chunk_in[c], 16)

            sp.dma_start(resid[:, 0, :], xt[:, 0, :]).then_inc(x_in, 16)
            sp.dma_start(resid[:, 1, :], xt[:, 1, :]).then_inc(x_in2, 16)
            sp.dma_start(grow[0:KD, :], norm_mix_g[0].rearrange("(k p) -> k p", p=P)).then_inc(small_in, 16)
            sp.dma_start(grow[KD:2 * KD, :], norm_ffn_g[0].rearrange("(k p) -> k p", p=P)).then_inc(small_in, 16)
            sp.dma_start(rel_sb[:, :], rel_bias).then_inc(small_in, 16)
            sp.dma_start(hot_sb[:, :], bucket_onehot).then_inc(small_in, 16)
            for c in range(6):
                load_chunk(c)
            for c in range(6, NCH):
                sp.wait_ge(unit_ps, LAST_UNIT[c - 6] + 1)
                load_chunk(c)
            for c, w, src in ((4, wp_sb, w_proj_sb), (5, wp_mb, w_proj_moba)):
                sp.wait_ge(unit_ps, LAST_UNIT[c] + 1)
                sp.dma_start(w, src[0].rearrange("(k p) n -> p k n", p=P)).then_inc(proj_in, 16)
            sp.wait_ge(unit_ps, LAST_UNIT[7] + 1)
            sp.dma_start(wo_sb, w_out[0].rearrange("(k p) n -> p k n", p=P)).then_inc(wout_in, 16)

            gu = w_gate_up[0].rearrange("e (k p) n -> e k p n", p=P)
            dn = w_down[0].rearrange("e (k c p) n -> e k p c n", p=P, c=2)

            def load_slot(e, s):
                if s < KD:
                    src = gu[e, s] if isinstance(e, int) else gu[bass.ds(e, 1), s].rearrange("o p n -> p (o n)")
                    sp.dma_start(ring[:, s, :], src).then_inc(slot_in[s], 16)
                else:
                    dst = ring[:, s, :].rearrange("p (c n) -> p c n", c=2)
                    src = (dn[e, s - KD] if isinstance(e, int)
                           else dn[bass.ds(e, 1), s - KD].rearrange("o p c n -> p (o c) n"))
                    sp.dma_start(dst, src).then_inc(slot_in[s], 16)

            for s in (4, 5, 6, 7):
                if s == 4:
                    sp.wait_ge(unit_ps, LAST_UNIT[9] + 1)
                load_slot(0, s)
            sp.wait_ge(out_ps, 8)
            for s in (8, 9, 10, 11):
                load_slot(0, s)
            sp.wait_ge(out_ps, 12)
            for s in (0, 1, 2, 3):
                load_slot(0, s)

            def experts(e0, done):
                with sp.Fori(e0, E) as e:
                    for s in range(RING):
                        sp.wait_ge(slot_used, (e + done) * RING + (s + 1 - RING))
                        load_slot(e, s)

            experts(1, 0)
            more_passes(sp, lambda r: experts(0, r * E))
            sp.wait_ge(out_rd, 1)
            sp.dma_start(out[0].rearrange("(t p) d -> p t d", p=P)[:, 0, :], scaled[:, 0, :]).then_inc(out_done, 16)
            sp.wait_ge(out_rd, 2)
            sp.dma_start(out[0].rearrange("(t p) d -> p t d", p=P)[:, 1, :], scaled[:, 1, :]).then_inc(out_done, 16)
            sp.wait_ge(out_done, 32)

        @block.gpsimd
        def _(pool):
            steps = [0]

            def link(ins):
                steps[0] += 1
                ins.then_inc(pool_step, 1)
                pool.wait_ge(pool_step, steps[0])

            link(nc.gpsimd.memset(ident[:, :], 0.0))
            nc.gpsimd.affine_select(out=ident[:, :], in_=ident[:, :], compare_op=ALU.not_equal, fill=1.0, base=0,
                                    pattern=[[-1, P]], channel_multiplier=1).then_inc(consts, 1)
            nc.gpsimd.memset(neg_one[:, :], -1.0).then_inc(consts, 1)
            link(nc.gpsimd.memset(neg_tri[:, :], -1.0))
            nc.gpsimd.affine_select(out=neg_tri[:, :], in_=neg_tri[:, :], compare_op=ALU.is_ge, fill=0.0, base=0,
                                    pattern=[[-1, P]], channel_multiplier=1).then_inc(consts, 1)
            nc.gpsimd.memset(ones_bf[:, :], 1.0).then_inc(consts2, 1)
            link(nc.gpsimd.memset(before[:, :], 1.0))
            nc.gpsimd.affine_select(out=before[:, :], in_=before[:, :], compare_op=ALU.is_gt, fill=0.0, base=0,
                                    pattern=[[1, P]], channel_multiplier=-1).then_inc(consts2, 1)
            nc.gpsimd.iota(slot_no[:, :, :], pattern=[[0, 2 * NT], [1, SLOTS]], base=0, channel_multiplier=0,
                           allow_small_or_imprecise_dtypes=True).then_inc(consts2, 1)
            nc.gpsimd.iota(eno[:, :], pattern=[[1, E]], base=0, channel_multiplier=0,
                           allow_small_or_imprecise_dtypes=True).then_inc(consts2, 1)
            link(nc.gpsimd.memset(expert_row[:, :], 0.0))
            for a in range(3):
                ins = nc.gpsimd.affine_select(out=expert_row[:, :], in_=expert_row[:, :], compare_op=ALU.not_equal,
                                              fill=1.0, base=-a * E, pattern=[[-1, E + 1]], channel_multiplier=1)
                if a < 2:
                    link(ins)
            link(ins)

            pool.wait_ge(u_rd, 1)
            pool.dma_start(u_dram, u_sb[:, :]).then_inc(u_out, 16)
            pool.wait_ge(u_out, 16)
            pool.dma_start(bias[:, :, :], bass.AP(tensor=u_dram.tensor, offset=0, ap=[[1, P], [UW, HMB], [1, T]])
                          ).then_inc(bias_in, 16)

            def diagonal(t):
                return t.rearrange("p (b c) -> p b c", b=3)[:, 0:3:2, :]

            def mask(t, ready):
                nc.gpsimd.affine_select(out=diagonal(t), in_=diagonal(t), compare_op=ALU.is_gt, fill=0.0, base=0,
                                        pattern=[[0, 2], [1, P]], channel_multiplier=-1).then_inc(ready, 1)

            for s in range(HSB + 1):
                if s < HSB:
                    pool.wait_ge(softplus, s + 1)
                    mask(att_s[:, s % 2, :], keep_rd)
                if s >= 1:
                    pool.wait_ge(weight_raw, s)
                    mask(att_w[:, (s - 1) % 2, :], weights_rd)

            def experts(done, r):
                base = 0 if r is None else r * (E + 1)
                with pool.Fori(0, E) as e:
                    pool.wait_ge(gathered, e + (base + 1))
                    nc.gpsimd.tensor_copy(expert_sel[:, :], expert_row[:, bass.ds(e, 1)].to_broadcast([3 * E, SLOTS])
                                          ).then_inc(sel_rd, 1)

            experts(0, None)
            more_passes(pool, lambda r: experts(r * E, r))

        @block.scalar
        def _(act):
            steps = [0]

            def link(ins):
                steps[0] += 1
                ins.then_inc(act_step, 1)
                act.wait_ge(act_step, steps[0])

            def columns(n, first_bank, g0):
                for k in (2, 3, 6, 7):
                    act.wait_ge(trans_ps, n * KD + 2 * (k // 2) + 2)
                    src = bank[first_bank + k // 2][:, (k % 2) * T:(k % 2) * T + T]
                    scale = 1.0 if g0 is None else gcol[:, g0 + k:g0 + k + 1]
                    nc.scalar.activation(colsT[:, k, :], src, ACT.Copy, scale=scale).then_inc(cols_act, 1)

            def squares(t, col):
                nc.scalar.activation(scaled[:, t, :], resid[:, t, :], ACT.Square,
                                     accum_out=stat[:, col + t:col + t + 1]).then_inc(ssq, 1)

            act.wait_ge(consts, 1)
            nc.scalar.activation(stat[:, 59:60], ident[:, 0:1], ACT.Sqrt)
            for t, arrived in enumerate((x_in, x_in2)):
                act.wait_ge(arrived, 16)
                squares(t, 0)
            act.wait_ge(rms_var, 1)
            nc.scalar.activation(stat[:, 4:6], stat[:, 2:4], ACT.Sqrt).then_inc(rms_std, 1)

            act.wait_ge(gcol_rd, 1)
            columns(0, 2, 0)
            for a in range(3):
                act.dma_start(gates[a * E:(a + 1) * E, 0, :], b_gate_up[0]).then_inc(late_in, 16)
            act.dma_start(router_w[:, :, :], w_router[0].rearrange("(k p) e -> p k e", p=P)).then_inc(late_in, 16)
            act.dma_start(b_rout[:, :], b_router[0].rearrange("(e o) -> e o", o=1)).then_inc(late_in, 16)
            act.dma_start(gfin[:, :], norm_final_g.rearrange("(o d) -> o d", o=1).to_broadcast([P, D])
                          ).then_inc(late_in, 16)

            def evacuate(u):
                kind, c, j = units[u]
                act.wait_ge(unit_ps, u + 1)
                src = bank[u % 2]
                if kind == "T":
                    row = {Q_SB: 0, K_SB: 4, Q_MB: 8, K_MB: 12}[c] + j
                    dst, src = qkT[:, row, :], src[:, 0:T]
                    scale = SCALE if c in (Q_SB, Q_MB) else 1.0
                elif c in (V_SB, V_MB):
                    dst, src, scale = values[:, j, (c == V_MB) * CH:(c == V_MB) * CH + CH], src[:, :], 1.0
                else:
                    if c == 6 and j == 0:
                        act.wait_ge(piece_d, 1)
                    dst, src, scale = gates[:, j, (c - 6) * CH:(c - 5) * CH], src[:, :], 1.0
                nc.scalar.activation(dst, src, ACT.Copy, scale=scale).then_inc(unit_rd, 1)

            for u in range(lead):
                evacuate(u)
            for s in range(NH + 1):
                if s < HSB:
                    act.wait_ge(z_ps, s + 1)
                    link(nc.scalar.activation(att_a[:, s % 2, :], bank[2 + s % 3][:, 0:TRI], ACT.Abs))
                    if s == 0:
                        act.wait_ge(u_out, 16)
                    if s >= 2:
                        act.wait_ge(softplus, s - 1)
                    link(nc.scalar.activation(att_e[:, s % 2, :], att_a[:, s % 2, :], ACT.Exp, scale=-1.0))
                    nc.scalar.activation(att_e[:, s % 2, :], att_e[:, s % 2, :], ACT.Ln, bias=1.0).then_inc(ln_rd, 1)
                elif s < NH:
                    b = s % 2
                    act.wait_ge(score_rd, s - HSB + 1)
                    for q, (c0, c1) in enumerate(((0, P), (P, TRI))):
                        nc.scalar.activation(att_s[:, b, c0:c1], att_s[:, b, c0:c1], ACT.Exp, bias=nmx[:, b, q:q + 1],
                                             accum_out=rs[:, b, q:q + 1]).then_inc(prob_raw, 1)
                if s < NH:
                    evacuate(fill_at[s])
                h = s - 1
                if h >= 0:
                    act.wait_ge(mid_ps, h + 1)
                    if h >= 2:
                        act.wait_ge(pv_ps, h - 1)
                    if h < HSB:
                        nc.scalar.activation(att_w[:, h % 2, :], bank[2 + h % 3][:, 0:TRI], ACT.Exp
                                             ).then_inc(weight_raw, 1)
                    else:
                        nc.scalar.activation(att_w[:, h % 2, :], bank[6][:, 0:TRI], ACT.Copy).then_inc(probT_rd, 1)
                if s in second_at:
                    evacuate(second_at[s])
            act.wait_ge(unit_rd, NU)
            for t in range(NT):
                nc.scalar.activation(gates[:, t, :], gates[:, t, :], ACT.Sigmoid).then_inc(sigm_rd, 1)

            act.wait_ge(pv_ps, NH)
            act.dma_start(bdown_sb, b_down[0]).then_inc(late_in, 16)

            columns(1, 4, None)
            nc.scalar.activation(stat[:, 58:59], stat[:, 6:7], ACT.Sqrt)
            for t in range(NT):
                act.wait_ge(hres_rd, 2 * (t + 1))
                act.wait_ge(trans_ps, 2 * KD)
                squares(t, 8)
            act.wait_ge(rms_var, 2)
            nc.scalar.activation(stat[:, 12:14], stat[:, 10:12], ACT.Sqrt).then_inc(rms_std, 1)
            nc.scalar.activation(stat[:, 57:58], stat[:, 6:7], ACT.Exp)
            columns(2, 4, KD)
            nc.scalar.activation(pieces[0], scaled[:, :, :], ACT.Copy).then_inc(piece_rd, 1)
            act.wait_ge(logit_ps, 1)
            act.wait_ge(late_in, 16 * 7)
            nc.scalar.activation(logitT, bank[0][0:E, 0:T], ACT.Identity, bias=b_rout[:, 0:1]).then_inc(logit_rd, 1)
            act.wait_ge(piece_d, 2)
            nc.scalar.activation(pieces[1], res2, ACT.Copy).then_inc(piece_rd, 1)
            act.wait_ge(top_rd, 1)
            for t in range(NT):
                nc.scalar.activation(topp[:, t, 0:TOP_K], top[:, t, 0:TOP_K], ACT.Exp, bias=stat[:, 16 + t:17 + t],
                                     accum_out=stat[:, 18 + t:19 + t]).then_inc(pexp, 1)
            act.wait_ge(gateT_ps, 1)
            nc.scalar.activation(gateT, bank[1][0:E, 0:T], ACT.Copy).then_inc(gateT_rd, 1)
            act.wait_ge(piece_d, 3)
            nc.scalar.activation(pieces[2], res2, ACT.Copy).then_inc(piece_rd, 1)

            def experts(done):
                with act.Fori(0, E) as e:
                    nc.scalar.activation(stat[:, 61:62], stat[:, 6:7], ACT.Sigmoid)
                    act.wait_ge(gT_ps, e + (done + 1))
                    nc.scalar.activation(scatter_w[:, :, :], bank[6][:, 0:T].rearrange("p (t s) -> p t s", t=NT),
                                         ACT.Copy).then_inc(gT_rd, 1)
                    act.wait_ge(gate_rd, e + (done + 1))
                    nc.scalar.activation(sig_t, gate_t, ACT.Sigmoid, scale=SWIGLU_ALPHA).then_inc(sig_rd, 1)
                    act.wait_ge(hT_ps, e + (done + 1))
                    nc.scalar.activation(hT[:, :, :], bank[6][:, :].rearrange("p (c s) -> p c s", c=4), ACT.Copy
                                         ).then_inc(hT_rd, 1)
                    act.wait_ge(slot_used, (e + (done + 1)) * RING)
                    nc.scalar.activation(y_t, bank[6][:, :], ACT.Copy).then_inc(y_rd, 1)

            experts(0)
            more_passes(act, lambda r: experts(r * E))
            nc.scalar.activation(stat[:, 56:57], stat[:, 6:7], ACT.Sqrt)
            for t in range(NT):
                act.wait_ge(hres_rd, 5 + t)
                squares(t, 20)
            act.wait_ge(rms_var, 3)
            nc.scalar.activation(stat[:, 24:26], stat[:, 22:24], ACT.Sqrt).then_inc(rms_std, 1)

        @block.vector
        def _(dve):
            steps = [0]
            V = nc.vector

            def link(ins):
                steps[0] += 1
                ins.then_inc(dve_step, 1)
                dve.wait_ge(dve_step, steps[0])

            def variance(col, n):
                dve.wait_ge(ssq, 2 * n)
                V.tensor_scalar(stat[:, col + 2:col + 4], stat[:, col:col + 2], 1.0 / D, RMS_EPS, ALU.mult, ALU.add
                                ).then_inc(rms_var, 1)
                dve.wait_ge(rms_std, n)
                link(V.reciprocal(stat[:, col + 6:col + 8], stat[:, col + 4:col + 6]))

            def scale_rows(col):
                for t in range(NT):
                    V.tensor_scalar(scaled[:, t, :], resid[:, t, :], stat[:, col + 6 + t:col + 7 + t], None, ALU.mult
                                    ).then_inc(scaled_rd, 1)

            def columns(n, first_bank, g0):
                for k in (0, 1, 4, 5):
                    dve.wait_ge(trans_ps, n * KD + 2 * (k // 2) + 2)
                    src = bank[first_bank + k // 2][:, (k % 2) * T:(k % 2) * T + T]
                    if g0 is None:
                        V.tensor_copy(colsT[:, k, :], src).then_inc(cols_rd, 1)
                    else:
                        V.tensor_scalar(colsT[:, k, :], src, gcol[:, g0 + k:g0 + k + 1], None, ALU.mult
                                        ).then_inc(cols_rd, 1)

            dve.wait_ge(gcol_ps, 1)
            V.tensor_copy(gcol[:, :], bank[6][:, 0:2 * KD]).then_inc(gcol_rd, 1)
            dve.wait_ge(gcol_rd, 1)
            variance(0, 1)
            scale_rows(0)
            columns(0, 2, 0)
            dve.wait_ge(u_ps, 1)
            link(V.tensor_copy(u_sb[:, :], bank[7][0:HMB, 0:UW]))
            V.memset(u_sb[:, 0:P - 1], MASKED).then_inc(u_rd, 1)

            dve.wait_ge(late_in, 16 * 6)
            whole, rest = gates[0:3 * E, 0, :], gates[0:3 * E, 1, :]
            link(V.tensor_copy(bgu[:, :], whole))
            link(V.tensor_tensor(rest, whole, bgu[:, :], ALU.subtract))
            link(V.tensor_copy(bgu[E:2 * E, :], gates[E:2 * E, 1, :]))
            link(V.tensor_copy(bgu[2 * E:3 * E, :], gates[2 * E:3 * E, 1, :]))
            link(V.tensor_tensor(gates[2 * E:3 * E, 0, :], gates[2 * E:3 * E, 1, :], bgu[2 * E:3 * E, :],
                                 ALU.subtract))
            V.tensor_copy(bgu[2 * E:3 * E, :], gates[2 * E:3 * E, 0, :]).then_inc(piece_d, 1)

            dve.wait_ge(bias_in, 16)
            for s in range(NH + 2):
                b = s % 2
                if s < HSB:
                    z = bank[2 + s % 3][:, 0:TRI]
                    dve.wait_ge(z_ps, s + 1)
                    dve.wait_ge(ln_rd, s + 1)
                    if s >= 2:
                        dve.wait_ge(mid_ps, s - 1)
                    V.scalar_tensor_tensor(out=att_s[:, b, :], in0=z, scalar=0.0, in1=att_e[:, b, :], op0=ALU.max,
                                           op1=ALU.add).then_inc(softplus, 1)
                elif s < NH:
                    h = s - HSB
                    z = bank[2 + s % 3]
                    dve.wait_ge(z_ps, s + 1)
                    dve.wait_ge(mid_ps, s - 1)
                    V.tensor_tensor(att_s[:, b, 0:P], z[:, 0:P], bias[:, h, P - 1::-1], ALU.add)
                    link(V.tensor_tensor(att_s[:, b, P:TRI], z[:, P:TRI], bias[:, h, ::-1], ALU.add))
                    V.reduce_max(mx[:, b, 0:1], att_s[:, b, 0:P], AX_X)
                    link(V.reduce_max(mx[:, b, 1:2], att_s[:, b, P:TRI], AX_X))
                    V.tensor_scalar(nmx[:, b, :], mx[:, b, :], -1.0, None, ALU.mult).then_inc(score_rd, 1)
                    dve.wait_ge(prob_raw, 2 * (h + 1))
                    link(V.reciprocal(rr[:, b, :], rs[:, b, :]))
                    for q, (c0, c1) in enumerate(((0, P), (P, TRI))):
                        V.tensor_scalar(att_s[:, b, c0:c1], att_s[:, b, c0:c1], rr[:, b, q:q + 1], None, ALU.mult
                                        ).then_inc(prob_rd, 1)
                h = s - 2
                if h >= 1 and h % 2 == 1:
                    pair = h // 2
                    dve.wait_ge(pv_ps, h + 1)
                    V.tensor_copy(yT[:, pair, :], bank[5 + 2 * (pair % 2)][:, 0:T]).then_inc(pv_rd, 1)

            dve.wait_ge(sigm_rd, NT)
            for m in range(2):
                for t in range(NT):
                    for c in range(2):
                        n = 4 * m + 2 * t + c
                        dve.wait_ge(out_ps, n + 1)
                        g = gates[:, t, m * D + c * CH:m * D + (c + 1) * CH]
                        link(V.tensor_tensor(g, g, bank[n % 4][:, :], ALU.mult))
                        if m == 0:
                            V.tensor_copy(stat[:, 60:61], stat[:, 6:7]).then_inc(merged, 1)
                        else:
                            V.tensor_tensor(scaled[:, t, c * CH:(c + 1) * CH], gates[:, t, c * CH:(c + 1) * CH], g,
                                            ALU.add).then_inc(merged, 1)
            columns(1, 4, None)
            for t in range(NT):
                for c in range(2):
                    dve.wait_ge(out_ps, 8 + 2 * t + c + 1)
                    part = resid[:, t, c * CH:(c + 1) * CH]
                    V.tensor_tensor(part, part, bank[2 * t + c][:, :], ALU.add).then_inc(hres_rd, 1)
            variance(8, 2)
            scale_rows(8)
            columns(2, 4, KD)
            dve.wait_ge(piece_rd, 1)
            V.tensor_tensor(res2, scaled[:, :, :], pieces[0], ALU.subtract).then_inc(piece_d, 1)

            dve.wait_ge(logit2_ps, 1)
            link(V.tensor_copy(rout[:, :, :], bank[1][:, 0:NT * E].rearrange("p (t e) -> p t e", t=NT)))
            for t in range(NT):
                link(V.max(out=top[:, t, :], in_=rout[:, t, :]))
                link(V.max_index(out=topi[:, t, :], in_max=top[:, t, :], in_values=rout[:, t, :]))
            V.tensor_scalar(stat[:, 16:18], top[:, :, 0:1].rearrange("p t o -> p (t o)"), -1.0, None, ALU.mult
                            ).then_inc(top_rd, 1)
            dve.wait_ge(consts2, 4)
            link(V.tensor_copy(topf[:, :, :], topi[:, :, :]))
            by_choice = [P, NT, TOP_K, E]
            link(V.tensor_tensor(chosen, eno[:, :].rearrange("p (a b e) -> p a b e", a=1, b=1).to_broadcast(by_choice),
                                 topf[:, :, 0:TOP_K].rearrange("p t (j o) -> p t j o", o=1).to_broadcast(by_choice),
                                 ALU.is_equal))
            link(V.reduce_sum(sel[:, :, :], chosen.rearrange("p t j e -> p t e j"), AX_X))
            V.tensor_copy(selb[:, :, :], sel[:, :, :]).then_inc(routed, 1)
            dve.wait_ge(piece_rd, 2)
            V.tensor_tensor(res2, res2, pieces[1], ALU.subtract).then_inc(piece_d, 1)
            dve.wait_ge(pexp, 2)
            link(V.reciprocal(stat[:, 34:36], stat[:, 18:20]))
            for t in range(NT):
                link(V.tensor_scalar(topp[:, t, 0:TOP_K], topp[:, t, 0:TOP_K], stat[:, 34 + t:35 + t], None,
                                     ALU.mult))
            link(V.tensor_tensor(chosen, chosen,
                                 topp[:, :, 0:TOP_K].rearrange("p t (j o) -> p t j o", o=1).to_broadcast(by_choice),
                                 ALU.mult))
            V.reduce_sum(gate_w[:, :, :], chosen.rearrange("p t j e -> p t e j"), AX_X).then_inc(weighted, 1)
            dve.wait_ge(weighted, 1)
            link(V.memset(gate_p[:, :, :], 0.0))
            link(V.memset(rank[:, :, :], -1.0))
            link(V.tensor_copy(gate_p[:, :, 0:E], gate_w[:, :, :]))
            dve.wait_ge(rank_ps, 1)
            ranks = bank[2][:, 0:NT * E].rearrange("p (t e) -> p t e", t=NT)
            link(V.scalar_tensor_tensor(out=pick[:, :, :], in0=ranks, scalar=1.0, in1=sel[:, :, :], op0=ALU.add,
                                        op1=ALU.mult))
            link(V.tensor_scalar(rank[:, :, 0:E], pick[:, :, :], -1.0, None, ALU.add))
            link(V.reduce_max(cnt_f[:, :], bank[2][:, NT * E:NT * E + E], AX_X))
            V.tensor_copy(cnt_i[:, :], cnt_f[:, :]).then_inc(count_rd, 1)

            def one_hots(col):
                return V.tensor_tensor(onehot[:, :, :], slot_no[:, :, 0:SLOTS],
                                       rank[:, :, bass.ds(col, 1)].to_broadcast([P, NT, SLOTS]), ALU.is_equal)

            def take(bank7):
                return V.tensor_tensor(xeT, bank7.rearrange("p (k s) -> p k s", k=KD),
                                       gcol[:, KD:2 * KD].rearrange("p (k o) -> p k o", o=1)
                                       .to_broadcast([P, KD, SLOTS]), ALU.mult)

            def experts(done, r):
                base = 0 if r is None else r * (E + 1)
                passes = 0 if r is None else r
                if r is not None:
                    dve.wait_ge(scattered, r)
                    V.tensor_scalar(slot_no[:, :, :], slot_no[:, :, :], float(SLOTS), None, ALU.add
                                    ).then_inc(pass_base, 1)
                    dve.wait_ge(pass_base, r)
                V.memset(y_t, 0.0).then_inc(y_rd, 1)
                V.memset(scatter_w[:, :, :], 0.0).then_inc(gT_rd, 1)
                one_hots(0).then_inc(onehot_rd, 1)
                dve.wait_ge(gathered, base + 1)
                take(bank[7][:, :]).then_inc(xe_rd, 1)
                with dve.Fori(0, E) as e:
                    dve.wait_ge(gathered, e + (base + 1))
                    one_hots(e + 1).then_inc(onehot_rd, 1)
                    V.tensor_tensor(onehot_w[:, :, :], slot_no[:, :, :],
                                    rank[:, :, bass.ds(e, 1)].to_broadcast([P, NT, P]), ALU.is_equal
                                    ).then_inc(pass_step, 1)
                    dve.wait_ge(pass_step, e * 3 + (done * 3 + 1))
                    dve.wait_ge(gT_rd, e + (base + 1))
                    V.tensor_tensor(onehot_g[:, :, :], onehot_w[:, :, :],
                                    gate_p[:, :, bass.ds(e, 1)].to_broadcast([P, NT, P]), ALU.mult
                                    ).then_inc(weighted_rd, 1)
                    dve.wait_ge(slot_used, (e + done) * RING + KD)
                    V.tensor_scalar(gate_t, bank[4][:, :], SWIGLU_LIMIT, None, ALU.min).then_inc(gate_rd, 1)
                    V.tensor_scalar(up_t, bank[5][:, :], SWIGLU_LIMIT, -SWIGLU_LIMIT, ALU.min, ALU.max
                                    ).then_inc(pass_step, 1)
                    dve.wait_ge(sig_rd, e + (done + 1))
                    V.tensor_tensor(sig_t, sig_t, gate_t, ALU.mult).then_inc(pass_step, 1)
                    dve.wait_ge(pass_step, e * 3 + (done * 3 + 3))
                    V.scalar_tensor_tensor(out=h_t, in0=up_t, scalar=1.0, in1=sig_t, op0=ALU.add, op1=ALU.mult
                                           ).then_inc(h_rd, 1)
                    dve.wait_ge(gathered, e + (base + 2))
                    take(bank[7][:, :]).then_inc(xe_rd, 1)
                dve.wait_ge(scattered, passes + 1)
                V.tensor_copy(stat[:, 62:63], stat[:, 6:7])

            experts(0, None)
            more_passes(dve, lambda r: experts(r * E, r))

            for t in range(NT):
                for c in range(2):
                    part = resid[:, t, c * CH:(c + 1) * CH]
                    ins = V.tensor_tensor(part, part, bank[2 * t + c][:, :], ALU.add)
                ins.then_inc(hres_rd, 1)
            variance(20, 3)
            for t in range(NT):
                V.scalar_tensor_tensor(out=scaled[:, t, :], in0=resid[:, t, :], scalar=stat[:, 26 + t:27 + t],
                                       in1=gfin[:, :], op0=ALU.mult, op1=ALU.mult).then_inc(out_rd, 1)

        @block.tensor
        def _(pe):
            mm = nc.tensor.matmul
            tp = nc.tensor.transpose
            pe.wait_ge(consts, 3)
            pe.wait_ge(small_in, 64)
            tp(bank[6][:, 0:2 * KD], grow[:, :], ident[0:2 * KD, 0:2 * KD]).then_inc(gcol_ps, 1)
            mm(bank[7][0:HMB, 0:UW], rel_sb[:, :], hot_sb[:, :], start=True, stop=True).then_inc(u_ps, 1)

            def transposes(first_bank):
                for k in range(KD):
                    for t in range(NT):
                        c0 = (k % 2) * T + t * P
                        ins = tp(bank[first_bank + k // 2][:, c0:c0 + P], scaled[:, t, k * P:(k + 1) * P], ident[:, :])
                    ins.then_inc(trans_ps, 1)

            pe.wait_ge(scaled_rd, 2)
            transposes(2)

            def column(n, k):
                pe.wait_ge(cols_act if (k // 2) % 2 else cols_rd, 4 * n + 2 * (k // 4) + k % 2 + 1)

            def unit(u):
                kind, c, j = units[u]
                pe.wait_ge(chunk_in[c], 16)
                if u >= 2:
                    pe.wait_ge(unit_rd, u - 1)
                w = chunk_w(c)
                for k in range(KD):
                    if u == 0:
                        column(0, k)
                    if kind == "T":
                        ins = mm(bank[u % 2][:, 0:T], w[:, k, j * P:(j + 1) * P], colsT[:, k, :], start=k == 0,
                                 stop=k == KD - 1)
                    else:
                        ins = mm(bank[u % 2][:, :], colsT[:, k, j * P:(j + 1) * P], w[:, k, :], start=k == 0,
                                 stop=k == KD - 1)
                ins.then_inc(unit_ps, 1)

            def scores(s):
                z = bank[2 + s % 3]
                if s >= 3:
                    if s - 3 < HSB:
                        pe.wait_ge(weight_raw, s - 2)
                    else:
                        pe.wait_ge(score_rd, s - 3 - HSB + 1)
                h = s % HSB
                r0 = HEAD_DIM * (h % 2)
                q = qkT[r0:r0 + HEAD_DIM, (0 if s < HSB else 8) + h // 2, :]
                k = qkT[r0:r0 + HEAD_DIM, (4 if s < HSB else 12) + h // 2, :]
                pe.wait_ge(unit_rd, unit_no[("T", K_SB if s < HSB else K_MB, h // 2)] + 1)
                if s < HSB:
                    mm(z[:, 0:T], k[:, 0:P], q, start=True, stop=True)
                    ins = mm(z[:, T:TRI], k[:, P:T], q[:, P:T], start=False, stop=True, skip_group_check=True)
                else:
                    mm(z[:, 0:P], q[:, 0:P], k[:, 0:P], start=True, stop=True)
                    ins = mm(z[:, P:TRI], q[:, P:T], k, start=True, stop=True)
                ins.then_inc(z_ps, 1)

            def middle(s):
                if s < HSB:
                    z = bank[2 + s % 3]
                    a = att_s[:, s % 2, :]
                    pe.wait_ge(keep_rd, s + 1)
                    mm(z[:, 0:T], neg_tri[:, :], a[:, 0:T], start=False, stop=True, skip_group_check=True)
                    mm(z[:, P:T], neg_one[:, :], a[:, T:TRI], start=False, stop=True, skip_group_check=True)
                    ins = mm(z[:, T:TRI], neg_tri[:, :], a[:, T:TRI], start=False, stop=True, skip_group_check=True)
                else:
                    pe.wait_ge(prob_rd, 2 * (s - HSB + 1))
                    if s > HSB:
                        pe.wait_ge(probT_rd, s - HSB)
                    for i in range(3):
                        ins = tp(bank[6][:, i * P:(i + 1) * P], att_s[:, s % 2, i * P:(i + 1) * P], ident[:, :])
                ins.then_inc(mid_ps, 1)

            def mix_values(s):
                if s < HSB:
                    pe.wait_ge(weights_rd, s + 1)
                else:
                    pe.wait_ge(probT_rd, s - HSB + 1)
                pair = s // 2
                if s == 0 or s == HSB:
                    pe.wait_ge(unit_rd, unit_no[("N", V_SB if s == 0 else V_MB, 1)] + 1)
                if pair >= 2:
                    pe.wait_ge(pv_rd, pair - 1)
                r0 = HEAD_DIM * (s % 2)
                o = bank[5 + 2 * (pair % 2)][r0:r0 + HEAD_DIM, :]
                v = values[:, :, s * HEAD_DIM:(s + 1) * HEAD_DIM]
                w = att_w[:, s % 2, :]
                mm(o[:, 0:T], v[:, 0, :], w[:, 0:T], start=True, stop=True)
                mm(o[:, P:T], v[:, 1, :], w[:, T:TRI], start=False, stop=True, skip_group_check=True).then_inc(pv_ps, 1)

            for u in range(lead):
                unit(u)
            for s in range(NH + 2):
                if s < NH:
                    scores(s)
                    unit(fill_at[s])
                if 1 <= s <= NH:
                    middle(s - 1)
                if s in second_at:
                    unit(second_at[s])
                if s >= 2:
                    mix_values(s - 2)

            for m, w in enumerate((wp_sb, wp_mb)):
                pe.wait_ge(proj_in, 16 * 2)
                pe.wait_ge(pv_rd, 4 * (m + 1))
                for t in range(NT):
                    for c in range(2):
                        n = 4 * m + 2 * t + c
                        if n == 0:
                            pe.wait_ge(unit_rd, NU)
                        if n >= 4:
                            pe.wait_ge(merged, n - 3)
                        for k in range(4):
                            ins = mm(bank[n % 4][:, :], yT[:, 4 * m + k, t * P:(t + 1) * P],
                                     w[:, k, c * CH:(c + 1) * CH], start=k == 0, stop=k == 3)
                        ins.then_inc(out_ps, 1)
            pe.wait_ge(merged, 8)
            transposes(4)
            pe.wait_ge(wout_in, 16)
            for t in range(NT):
                for c in range(2):
                    for k in range(KD):
                        if t == c == 0:
                            column(1, k)
                        ins = mm(bank[2 * t + c][:, :], colsT[:, k, t * P:(t + 1) * P], wo_sb[:, k, c * CH:(c + 1) * CH],
                                 start=k == 0, stop=k == KD - 1)
                    ins.then_inc(out_ps, 1)
            pe.wait_ge(scaled_rd, 4)
            transposes(4)
            pe.wait_ge(late_in, 16 * 7)
            pe.wait_ge(hres_rd, 4)
            for k in range(KD):
                column(2, k)
                ins = mm(bank[0][0:E, 0:T], router_w[:, k, :], colsT[:, k, :], start=k == 0, stop=k == KD - 1)
            ins.then_inc(logit_ps, 1)
            pe.wait_ge(logit_rd, 1)
            for t in range(NT):
                ins = tp(bank[1][:, t * E:(t + 1) * E], logitT[:, t * P:(t + 1) * P], ident[0:E, 0:E])
            ins.then_inc(logit2_ps, 1)
            pe.wait_ge(routed, 1)
            rk = bank[2]
            mm(rk[:, 0:E], before[:, :], selb[:, 0, :], start=True, stop=True)
            mm(rk[:, E:2 * E], ones_bf[:, :], selb[:, 0, :], start=True, stop=False)
            mm(rk[:, E:2 * E], before[:, :], selb[:, 1, :], start=False, stop=True)
            for t in range(NT):
                ins = mm(rk[:, 2 * E:3 * E], ones_bf[:, :], selb[:, t, :], start=t == 0, stop=t == NT - 1)
            ins.then_inc(rank_ps, 1)
            pe.wait_ge(weighted, 1)
            for t in range(NT):
                ins = tp(bank[1][0:E, t * P:(t + 1) * P], gate_w[:, t, :], ident[:, :])
            ins.then_inc(gateT_ps, 1)
            pe.wait_ge(piece_rd, 3)

            def gather(count):
                pe.wait_ge(onehot_rd, count)
                for k in range(KD):
                    for i in range(3):
                        for t in range(NT):
                            n = i * NT + t
                            ins = mm(bank[7][:, k * SLOTS:(k + 1) * SLOTS], pieces[i][:, t, k * P:(k + 1) * P],
                                     onehot[:, t, :], start=n == 0, stop=n == 3 * NT - 1)
                ins.then_inc(gathered, 1)

            def scatter():
                for t in range(NT):
                    for c in range(2):
                        r = slice(SLOTS * c, SLOTS * (c + 1))
                        ins = mm(bank[2 * t + c][:, :], scatter_w[r, t, :], y_t[r, :], start=False, stop=True,
                                 skip_group_check=True)
                return ins

            def experts(done, r):
                base = 0 if r is None else r * (E + 1)
                gather(base + 1)
                if r is None:
                    pe.wait_ge(gateT_rd, 1)
                    pe.wait_ge(count_rd, 1)
                    for t in range(NT):
                        for c in range(2):
                            mm(bank[2 * t + c][:, :], gateT[:, t * P:(t + 1) * P], bdown_sb[:, c * CH:(c + 1) * CH], start=True,
                               stop=True)
                with pe.Fori(0, E) as e:
                    pe.wait_ge(sel_rd, e + (done + 1))
                    pe.wait_ge(xe_rd, e + (base + 1))
                    for i in range(2):
                        for c in range(2):
                            mm(bank[4 + i][SLOTS * c:SLOTS * (c + 1), :], expert_sel[:, :],
                               bgu[:, i * D + c * CH:i * D + (c + 1) * CH], start=True, stop=False)
                    for k in range(KD):
                        pe.wait_ge(slot_in[k], e * 16 + (done * 16 + 16))
                        for i in range(2):
                            for c in range(2):
                                ins = mm(bank[4 + i][SLOTS * c:SLOTS * (c + 1), :], xeT[:, k, :],
                                         ring[:, k, i * D + c * CH:i * D + (c + 1) * CH], start=False,
                                         stop=k == KD - 1)
                        ins.then_inc(slot_used, 1)
                        if k == 1:
                            pe.wait_ge(y_rd, e + (base + 1))
                            pe.wait_ge(gT_rd, e + (base + 1))
                            scatter()
                            pe.wait_ge(weighted_rd, e + (done + 1))
                            for t in range(NT):
                                ins = tp(bank[6][:, t * P:(t + 1) * P], onehot_g[:, t, :], ident[:, :])
                            ins.then_inc(gT_ps, 1)
                        if k == 4:
                            gather(e + (base + 2))
                    pe.wait_ge(gT_rd, e + (base + 2))
                    pe.wait_ge(h_rd, e + (done + 1))
                    for c in range(4):
                        ins = tp(bank[6][:, c * P:(c + 1) * P], h_t[:, c * P:(c + 1) * P], ident[:, :])
                    ins.then_inc(hT_ps, 1)
                    pe.wait_ge(hT_rd, e + (done + 1))
                    for s in range(4):
                        pe.wait_ge(slot_in[KD + s], e * 16 + (done * 16 + 16))
                        for j in range(2):
                            k = 2 * s + j
                            rows = hT[:, k % 4, SLOTS * (k // 4):SLOTS * (k // 4) + SLOTS]
                            for c in range(2):
                                ins = mm(bank[6][SLOTS * c:SLOTS * (c + 1), :], rows,
                                         ring[:, KD + s, j * D + c * CH:j * D + (c + 1) * CH], start=k == 0,
                                         stop=k == KD - 1)
                        ins.then_inc(slot_used, 1)
                pe.wait_ge(y_rd, base + (E + 1))
                pe.wait_ge(gT_rd, base + (E + 1))
                scatter().then_inc(scattered, 1)

            experts(0, None)
            more_passes(pe, lambda r: experts(r * E, r))


_INS = ['x', 'norm_mix_g', 'w_in', 'w_proj_sb', 'w_proj_moba', 'w_out', 'rel_bias', 'norm_ffn_g', 'w_router',
        'b_router', 'w_gate_up', 'b_gate_up', 'w_down', 'b_down', 'norm_final_g']


def kernel(**inputs):
    import concourse.bacc as _bacc
    from concourse.bass_utils import run_bass_kernel_spmd as _run

    nc = _bacc.Bacc("TRN2", target_bir_lowering=False, num_devices=1)
    arrays, args = {}, []
    held = {n: np.ascontiguousarray(inputs[n]) for n in _INS}
    held["bucket_onehot"] = bucket_rows(32, 3 * P)
    for name, a in held.items():
        arrays[f"in_{name}_dram"] = a
        args.append(nc.dram_tensor(f"in_{name}_dram", a.shape, mybir.dt.from_np(a.dtype), kind="ExternalInput").ap())
    out = nc.dram_tensor("out_0_dram", (1, 256, 1024), F32, kind="ExternalOutput").ap()
    hybrid_layer(nc, *args, out)
    r = _run(nc, [arrays], core_ids=[0])
    return r.results[0]["out_0_dram"]
```
